# Optimizing a Trainium2 kernel written in Bass

```python
import jax, jax.numpy as jnp
from jax import lax
import numpy as np

D_MODEL = 1024
BATCH = 1
SEQ = 512
DEPTH = 2

HEAD_DIM = 64
N_Q_A = 16
N_KV_A = 2
GROUP_A = N_Q_A // N_KV_A
WINDOW = 128
BLOCK = 128
N_H_B = 16
ROT_DIM = HEAD_DIM // 4
ROPE_THETA = 500000.0
D_FF = -(-8 * D_MODEL // (3 * 256)) * 256
N_MIXERS = 2
N_A = (DEPTH + 1) // 2
N_B = DEPTH // 2
QKV_A = (N_Q_A + 2 * N_KV_A) * HEAD_DIM
QKV_B = 3 * N_H_B * HEAD_DIM
EPS = 1e-6


def rmsnorm(x, gain):
    xf = x.astype(jnp.float32)
    y = xf * lax.rsqrt(jnp.mean(xf * xf, axis=-1, keepdims=True) + EPS)
    return (y * gain.astype(jnp.float32)).astype(x.dtype)

def partial_rope(x, positions):
    half = ROT_DIM // 2
    inv_freq = jnp.power(jnp.float32(ROPE_THETA), -jnp.arange(half, dtype=jnp.float32) * 2.0 / ROT_DIM)
    ang = positions.astype(jnp.float32)[:, :, None, None] * inv_freq
    cos, sin = jnp.cos(ang), jnp.sin(ang)
    xr = x[..., :ROT_DIM].astype(jnp.float32)
    x1, x2 = xr[..., :half], xr[..., half:]
    rot = jnp.concatenate([x1 * cos - x2 * sin, x2 * cos + x1 * sin], axis=-1).astype(x.dtype)
    return jnp.concatenate([rot, x[..., ROT_DIM:]], axis=-1)

def sliding_window_sink_attention(h, positions, w_qkv, q_gain, k_gain, sinks, w_o):
    B, S, _ = h.shape
    qkv = h @ w_qkv
    q, k, v = jnp.split(qkv, [N_Q_A * HEAD_DIM, (N_Q_A + N_KV_A) * HEAD_DIM], axis=-1)
    q = q.reshape(B, S, N_Q_A, HEAD_DIM)
    k = k.reshape(B, S, N_KV_A, HEAD_DIM)
    v = v.reshape(B, S, N_KV_A, HEAD_DIM)
    q = partial_rope(rmsnorm(q, q_gain), positions)
    k = partial_rope(rmsnorm(k, k_gain), positions)
    q = q.reshape(B, S, N_KV_A, GROUP_A, HEAD_DIM)
    pad = jnp.zeros((B, BLOCK, N_KV_A, HEAD_DIM), k.dtype)
    kp = jnp.concatenate([pad, k], axis=1)
    vp = jnp.concatenate([pad, v], axis=1)
    scale = HEAD_DIM ** -0.5
    q_idx = jnp.arange(BLOCK)[:, None] + BLOCK
    k_idx = jnp.arange(2 * BLOCK)[None, :]
    rel = q_idx - k_idx
    band = (rel >= 0) & (rel < WINDOW)
    sink_logit = sinks.astype(jnp.float32).reshape(1, N_KV_A, GROUP_A, 1, 1)

    def block_fn(i):
        start = i * BLOCK
        qb = lax.dynamic_slice_in_dim(q, start, BLOCK, axis=1)
        kb = lax.dynamic_slice_in_dim(kp, start, 2 * BLOCK, axis=1)
        vb = lax.dynamic_slice_in_dim(vp, start, 2 * BLOCK, axis=1)
        s = jnp.einsum('bqkgd,bskd->bkgqs', qb, kb).astype(jnp.float32) * scale
        valid = band & (start - BLOCK + k_idx >= 0)
        s = jnp.where(valid, s, -jnp.inf)
        sink_col = jnp.broadcast_to(sink_logit, s.shape[:-1] + (1,))
        p = jax.nn.softmax(jnp.concatenate([s, sink_col], axis=-1), axis=-1)[..., :-1]
        o = jnp.einsum('bkgqs,bskd->bqkgd', p.astype(vb.dtype), vb)
        return o.reshape(B, BLOCK, N_Q_A * HEAD_DIM)

    out = lax.map(block_fn, jnp.arange(S // BLOCK))
    out = jnp.moveaxis(out, 0, 1).reshape(B, S, N_Q_A * HEAD_DIM)
    return out @ w_o

def stick_breaking_attention(h, w_qkv, w_o):
    B, S, _ = h.shape
    qkv = h @ w_qkv
    q, k, v = jnp.split(qkv, 3, axis=-1)
    q = q.reshape(B, S, N_H_B, HEAD_DIM)
    k = k.reshape(B, S, N_H_B, HEAD_DIM)
    v = v.reshape(B, S, N_H_B, HEAD_DIM)
    scale = HEAD_DIM ** -0.5
    k_idx = jnp.arange(S)[None, :]

    def block_fn(i):
        start = i * BLOCK
        qb = lax.dynamic_slice_in_dim(q, start, BLOCK, axis=1)
        z = jnp.einsum('bqhd,bshd->bhqs', qb, k).astype(jnp.float32) * scale
        t_idx = start + jnp.arange(BLOCK)[:, None]
        strict = k_idx < t_idx
        log_beta = jax.nn.log_sigmoid(z)
        log_one_minus = jnp.where(strict, jax.nn.log_sigmoid(-z), 0.0)
        rc = lax.cumsum(log_one_minus, axis=3, reverse=True)
        after = jnp.pad(rc[..., 1:], ((0, 0), (0, 0), (0, 0), (0, 1)))
        a = jnp.where(strict, jnp.exp(log_beta + after), 0.0)
        o = jnp.einsum('bhqs,bshd->bqhd', a.astype(v.dtype), v)
        return o.reshape(B, BLOCK, N_H_B * HEAD_DIM)

    out = lax.map(block_fn, jnp.arange(S // BLOCK))
    out = jnp.moveaxis(out, 0, 1).reshape(B, S, N_H_B * HEAD_DIM)
    return out @ w_o

def swiglu(h, w_gate, w_up, w_down):
    return (jax.nn.silu(h @ w_gate) * (h @ w_up)) @ w_down

def first_inputs(seed: int = 0) -> dict:
    key = jax.random.key(seed)
    ks = jax.random.split(key, 20)
    f32 = jnp.float32
    nrm = lambda k, shape, s: jax.random.normal(k, shape, f32) * s
    x = jax.random.normal(ks[0], (BATCH, SEQ, D_MODEL), f32)
    c = jax.random.normal(ks[1], (BATCH, D_MODEL), f32)
    offset = jax.random.randint(ks[2], (BATCH, 1), 0, 4096, dtype=jnp.int32)
    positions = offset + jnp.arange(SEQ, dtype=jnp.int32)[None, :]
    return {
        'x': x,
        'c': c,
        'positions': positions,
        'ada_w': nrm(ks[3], (DEPTH, D_MODEL, 6 * D_MODEL), 0.5 * D_MODEL ** -0.5),
        'ada_b': nrm(ks[4], (DEPTH, 6 * D_MODEL), 0.01),
        'norm1_g': 1.0 + nrm(ks[5], (DEPTH, D_MODEL), 0.05),
        'norm2_g': 1.0 + nrm(ks[6], (DEPTH, D_MODEL), 0.05),
        'wqkv_a': nrm(ks[7], (N_A, D_MODEL, QKV_A), D_MODEL ** -0.5),
        'q_norm_a': 1.0 + nrm(ks[8], (N_A, HEAD_DIM), 0.05),
        'k_norm_a': 1.0 + nrm(ks[9], (N_A, HEAD_DIM), 0.05),
        'sinks_a': nrm(ks[10], (N_A, N_Q_A), 1.0),
        'wo_a': nrm(ks[11], (N_A, N_Q_A * HEAD_DIM, D_MODEL), (N_Q_A * HEAD_DIM) ** -0.5),
        'wqkv_b': nrm(ks[12], (N_B, D_MODEL, QKV_B), D_MODEL ** -0.5),
        'wo_b': nrm(ks[13], (N_B, N_H_B * HEAD_DIM, D_MODEL), (N_H_B * HEAD_DIM) ** -0.5),
        'w_gate': nrm(ks[14], (DEPTH, D_MODEL, D_FF), D_MODEL ** -0.5),
        'w_up': nrm(ks[15], (DEPTH, D_MODEL, D_FF), D_MODEL ** -0.5),
        'w_down': nrm(ks[16], (DEPTH, D_FF, D_MODEL), D_FF ** -0.5),
    }

def first_block(x, c, positions, ada_w, ada_b, norm1_g, norm2_g, wqkv_a, q_norm_a, k_norm_a,
              sinks_a, wo_a, wqkv_b, wo_b, w_gate, w_up, w_down):
    cond = jax.nn.silu(c)
    for i in range(DEPTH):
        mod = (cond @ ada_w[i] + ada_b[i])[:, None, :]
        sh1, sc1, g1, sh2, sc2, g2 = jnp.split(mod, 6, axis=-1)
        h = rmsnorm(x, norm1_g[i]) * (1.0 + sc1) + sh1
        j = i // N_MIXERS
        if i % N_MIXERS == 0:
            y = sliding_window_sink_attention(h, positions, wqkv_a[j], q_norm_a[j], k_norm_a[j],
                                              sinks_a[j], wo_a[j])
        else:
            y = stick_breaking_attention(h, wqkv_b[j], wo_b[j])
        x = x + g1 * y
        h = rmsnorm(x, norm2_g[i]) * (1.0 + sc2) + sh2
        x = x + g2 * swiglu(h, w_gate[i], w_up[i], w_down[i])
    return x


DEPTH_2 = 1

D_CONV = D_MODEL
CONV_A_WIDTH = 3
EXPAND = 2
D_INNER = EXPAND * D_MODEL
N_HEADS = D_INNER // HEAD_DIM
N_GROUPS = 4
D_STATE = 128
SSD_CONV_WIDTH = 4
CHUNK = 128
D_XBC = D_INNER + 2 * N_GROUPS * D_STATE
D_FF_2 = 2816
FFN_CONV_WIDTH = 3
N_IN = 2 * D_MODEL + 3 * D_CONV + D_INNER + D_XBC + N_HEADS
EPS_2 = 1e-5
DT_MIN = 1e-3
DT_MAX = 1e-1


def rmsnorm_2(x, w):
    xf = x.astype(jnp.float32)
    y = xf * lax.rsqrt(jnp.mean(xf * xf, axis=-1, keepdims=True) + EPS_2)
    return (y * w.astype(jnp.float32)).astype(x.dtype)

def causal_dwconv(x, w):
    k, c = w.shape
    return lax.conv_general_dilated(
        x, w[:, None, :].astype(x.dtype), window_strides=(1,), padding=[(k - 1, 0)],
        dimension_numbers=("NWC", "WIO", "NWC"), feature_group_count=c)

def ssd_chunked_scan(xh, dt, a, bmat, cmat):
    b, s, h, p = xh.shape
    g, n = bmat.shape[-2:]
    j = h // g
    c = s // CHUNK
    x_ = (xh.astype(jnp.float32) * dt[..., None]).reshape(b, c, CHUNK, g, j, p)
    log_a = jnp.moveaxis((dt * a).reshape(b, c, CHUNK, g, j), 2, -1)
    bc = bmat.astype(jnp.float32).reshape(b, c, CHUNK, g, n)
    cc = cmat.astype(jnp.float32).reshape(b, c, CHUNK, g, n)
    a_cum = jnp.cumsum(log_a, axis=-1)

    causal = jnp.tril(jnp.ones((CHUNK, CHUNK), dtype=bool))
    seg = a_cum[..., :, None] - a_cum[..., None, :]
    decay_in = jnp.exp(jnp.where(causal, seg, -jnp.inf))
    cb = jnp.einsum("bclgn,bcsgn->bcgls", cc, bc)
    y_diag = jnp.einsum("bcgjls,bcsgjp->bclgjp", cb[:, :, :, None] * decay_in, x_)

    decay_to_end = jnp.exp(a_cum[..., -1:] - a_cum)
    states = jnp.einsum("bclgn,bcgjl,bclgjp->bcgjpn", bc, decay_to_end, x_)
    chunk_decay = jnp.exp(a_cum[..., -1])

    def step(carry, inp):
        st, dec = inp
        return carry * dec[..., None, None] + st, carry

    init = jnp.zeros((b, g, j, p, n), jnp.float32)
    _, prev = lax.scan(step, init, (jnp.moveaxis(states, 1, 0), jnp.moveaxis(chunk_decay, 1, 0)))
    prev = jnp.moveaxis(prev, 0, 1)
    y_off = jnp.einsum("bclgn,bcgjpn,bcgjl->bclgjp", cc, prev, jnp.exp(a_cum))
    return (y_diag + y_off).reshape(b, s, h, p)

def gated_group_rmsnorm(y, z, w):
    bsz, s, d = y.shape
    yf = (y.astype(jnp.float32) * jax.nn.silu(z.astype(jnp.float32))).reshape(bsz, s, N_GROUPS, d // N_GROUPS)
    yf = yf * lax.rsqrt(jnp.mean(yf * yf, axis=-1, keepdims=True) + EPS_2)
    return (yf.reshape(bsz, s, d) * w.astype(jnp.float32)).astype(y.dtype)

def hybrid_mixer(u, w_in, conv_a_w, w_a_out, ssd_conv_w, ssd_conv_b, dt_bias, a_log,
                 d_skip, ssd_norm_w, w_s_out, w_o):
    bsz, s, _ = u.shape
    proj = u @ w_in
    sizes = [D_MODEL, D_MODEL, D_CONV, D_CONV, D_CONV, D_INNER, D_XBC, N_HEADS]
    offsets = np.cumsum(sizes)[:-1].tolist()
    gate_a, gate_s, b_a, c_a, v_a, z, xbc, dt_raw = jnp.split(proj, offsets, axis=-1)

    y_a = (b_a * causal_dwconv(c_a * v_a, conv_a_w)) @ w_a_out

    xbc = jax.nn.silu(causal_dwconv(xbc, ssd_conv_w) + ssd_conv_b)
    xs, bs, cs = jnp.split(xbc, [D_INNER, D_INNER + N_GROUPS * D_STATE], axis=-1)
    xh = xs.reshape(bsz, s, N_HEADS, HEAD_DIM)
    dt = jax.nn.softplus(dt_raw.astype(jnp.float32) + dt_bias.astype(jnp.float32))
    a = -jnp.exp(a_log.astype(jnp.float32))
    y = ssd_chunked_scan(xh, dt, a,
                         bs.reshape(bsz, s, N_GROUPS, D_STATE),
                         cs.reshape(bsz, s, N_GROUPS, D_STATE))
    y = y + d_skip.astype(jnp.float32)[:, None] * xh.astype(jnp.float32)
    y = y.reshape(bsz, s, D_INNER).astype(u.dtype)
    y_s = gated_group_rmsnorm(y, z, ssd_norm_w) @ w_s_out

    merged = jax.nn.sigmoid(gate_a) * y_a + jax.nn.sigmoid(gate_s) * y_s
    return merged @ w_o

def conv_gated_mlp(v, w_up, ffn_conv_w, ffn_conv_b, w_down):
    hv = v @ w_up
    h1, h3 = jnp.split(hv, 2, axis=-1)
    h1 = causal_dwconv(h1, ffn_conv_w) + ffn_conv_b
    return (jax.nn.silu(h1) * h3) @ w_down

def second_inputs(seed: int = 0) -> dict:
    key = jax.random.key(seed)
    ks = jax.random.split(key, 24)
    f32 = jnp.float32

    def nrm(k, shape, scale):
        return jax.random.normal(k, shape, f32) * scale

    dt0 = jnp.exp(jax.random.uniform(ks[9], (DEPTH_2, N_HEADS), f32)
                  * (np.log(DT_MAX) - np.log(DT_MIN)) + np.log(DT_MIN))
    dt_bias = dt0 + jnp.log(-jnp.expm1(-dt0))
    return {
        "x": nrm(ks[0], (BATCH, SEQ, D_MODEL), 1.0),
        "norm_mix_w": 1.0 + nrm(ks[1], (DEPTH_2, D_MODEL), 0.02),
        "w_in": nrm(ks[2], (DEPTH_2, D_MODEL, N_IN), D_MODEL ** -0.5),
        "conv_a_w": nrm(ks[3], (DEPTH_2, CONV_A_WIDTH, D_CONV), CONV_A_WIDTH ** -0.5),
        "w_a_out": nrm(ks[4], (DEPTH_2, D_CONV, D_MODEL), D_CONV ** -0.5),
        "ssd_conv_w": nrm(ks[5], (DEPTH_2, SSD_CONV_WIDTH, D_XBC), SSD_CONV_WIDTH ** -0.5),
        "ssd_conv_b": nrm(ks[6], (DEPTH_2, D_XBC), 0.02),
        "dt_bias": dt_bias,
        "a_log": jnp.log(jax.random.uniform(ks[7], (DEPTH_2, N_HEADS), f32, 1.0, 16.0)),
        "d_skip": 1.0 + nrm(ks[8], (DEPTH_2, N_HEADS), 0.02),
        "ssd_norm_w": 1.0 + nrm(ks[10], (DEPTH_2, D_INNER), 0.02),
        "w_s_out": nrm(ks[11], (DEPTH_2, D_INNER, D_MODEL), D_INNER ** -0.5),
        "w_o": nrm(ks[12], (DEPTH_2, D_MODEL, D_MODEL), D_MODEL ** -0.5),
        "norm_ffn_w": 1.0 + nrm(ks[13], (DEPTH_2, D_MODEL), 0.02),
        "w_up": nrm(ks[14], (DEPTH_2, D_MODEL, 2 * D_FF_2), D_MODEL ** -0.5),
        "ffn_conv_w": nrm(ks[15], (DEPTH_2, FFN_CONV_WIDTH, D_FF_2), FFN_CONV_WIDTH ** -0.5),
        "ffn_conv_b": nrm(ks[16], (DEPTH_2, D_FF_2), 0.02),
        "w_down": nrm(ks[17], (DEPTH_2, D_FF_2, D_MODEL), D_FF_2 ** -0.5),
        "final_norm_w": 1.0 + nrm(ks[18], (D_MODEL,), 0.02),
    }

def second_block(x, norm_mix_w, w_in, conv_a_w, w_a_out, ssd_conv_w, ssd_conv_b, dt_bias,
              a_log, d_skip, ssd_norm_w, w_s_out, w_o, norm_ffn_w, w_up, ffn_conv_w,
              ffn_conv_b, w_down, final_norm_w):
    h = x
    for l in range(DEPTH_2):
        u = rmsnorm_2(h, norm_mix_w[l])
        h = h + hybrid_mixer(u, w_in[l], conv_a_w[l], w_a_out[l], ssd_conv_w[l], ssd_conv_b[l],
                             dt_bias[l], a_log[l], d_skip[l], ssd_norm_w[l], w_s_out[l], w_o[l])
        v = rmsnorm_2(h, norm_ffn_w[l])
        h = h + conv_gated_mlp(v, w_up[l], ffn_conv_w[l], ffn_conv_b[l], w_down[l])
    return rmsnorm_2(h, final_norm_w)


def setup_inputs(seed=0):
    out = dict(first_inputs(seed))
    for name, value in second_inputs(seed + 1).items():
        if name != "x":
            out[name + "_2"] = value
    return out


def reference(
    x, c, positions, ada_w, ada_b, norm1_g, norm2_g, wqkv_a, q_norm_a, k_norm_a, sinks_a, wo_a,
    wqkv_b, wo_b, w_gate, w_up, w_down, norm_mix_w_2, w_in_2, conv_a_w_2, w_a_out_2,
    ssd_conv_w_2, ssd_conv_b_2, dt_bias_2, a_log_2, d_skip_2, ssd_norm_w_2, w_s_out_2, w_o_2,
    norm_ffn_w_2, w_up_2, ffn_conv_w_2, ffn_conv_b_2, w_down_2, final_norm_w_2,
):
    x = first_block(
        x, c, positions, ada_w, ada_b, norm1_g, norm2_g, wqkv_a, q_norm_a, k_norm_a, sinks_a,
        wo_a, wqkv_b, wo_b, w_gate, w_up, w_down,
    )
    return second_block(
        x, norm_mix_w_2, w_in_2, conv_a_w_2, w_a_out_2, ssd_conv_w_2, ssd_conv_b_2, dt_bias_2,
        a_log_2, d_skip_2, ssd_norm_w_2, w_s_out_2, w_o_2, norm_ffn_w_2, w_up_2, ffn_conv_w_2,
        ffn_conv_b_2, w_down_2, final_norm_w_2,
    )


_drawn_inputs = setup_inputs


def setup_inputs(seed=0):
    import zlib

    import numpy as np

    out = dict(_drawn_inputs(seed))
    spreads = {}
    factors = {'ada_b': 2.677,
     'norm1_g': 3.039,
     'q_norm_a': 8.0,
     'k_norm_a': 8.0,
     'sinks_a': 6.577,
     'norm_mix_w_2': 2.67,
     'ssd_conv_b_2': 16.14,
     'd_skip_2': 200.0,
     'ssd_norm_w_2': 115.284,
     'norm_ffn_w_2': 19.622,
     'ffn_conv_b_2': 27.287,
     'final_norm_w_2': 21.705}
    for name, (base, spread) in spreads.items():
        noise = np.random.default_rng([zlib.crc32(name.encode()), seed]).standard_normal(out[name].shape)
        drawn = base * np.exp(spread * noise) if base else spread * noise
        out[name] = __import__('jax').numpy.asarray(drawn.astype(out[name].dtype))
    for name, factor in factors.items():
        out[name] = (out[name] * factor).astype(out[name].dtype)
    return out
```

```python
from collections import deque
from contextlib import ExitStack

import numpy as np
import concourse.bass as bass
from concourse import mybir

F = mybir.dt.float32
R = mybir.dt.float32r
I32 = mybir.dt.int32
ACT = mybir.ActivationFunctionType
ALU = mybir.AluOpType

P = 128
S = 512
D = 1024
KD = D // P
DFF = 2816
KF = DFF // P
HALF = 12
UNITS = 361
NRAW = 3
NW = 3
NSLOT = 31
NADA = 8
NEG = -1.0e30
EPS1 = 1e-6
EPS2 = 1e-5


def spans(parts):
    out, at = {}, 0
    for name, n in parts:
        out[name] = (at, n)
        at += n
    return out, at


CONST, NCONST = spans([
    ("ident", 128), ("tri", 128), ("nones", 128), ("maskA", 256), ("capB", 128), ("maskB", 128),
    ("maskS", 128), ("perm", 128), ("heads", 2), ("one", 1), ("invf", 1), ("sgn", 1), ("half", 8),
])
VEC, NVEC = spans([
    ("c", 8), ("ada_b", 96), ("norm1", 16), ("norm2", 16), ("qg", 1), ("kg", 1), ("sinks", 16),
    ("mix", 8), ("ffn", 8), ("fin", 8), ("caw", 24), ("scw", 96), ("scb", 24), ("snw", 16),
    ("fcw", 66), ("fcb", 22), ("skip", 16), ("dtb", 1), ("alog", 1),
])


def constants():
    c = np.zeros((P, NCONST), np.float32)

    def put(name, a):
        at, n = CONST[name]
        c[:, at:at + n] = a

    i = np.arange(P)
    put("ident", np.eye(P))
    put("tri", np.where(i[:, None] >= i[None, :], -1.0, 0.0))
    put("nones", -1.0)
    j = np.arange(2 * P)
    put("maskA", np.where((j[None, :] > i[:, None]) & (j[None, :] <= i[:, None] + P), 0.0, NEG))
    put("capB", np.where(i[:, None] < i[None, :], 3.0e38, 0.0))
    put("maskB", np.where(i[:, None] < i[None, :], 1.0, 0.0))
    put("maskS", np.where(i[:, None] <= i[None, :], 1.0, 0.0))
    perm = np.zeros((P, P))
    inv = np.power(500000.0, -np.arange(8) * 2.0 / 16)
    invf, sgn = np.zeros(P), np.zeros(P)
    for b in (0, 64):
        for r in range(8):
            perm[b + 8 + r, b + r] = 1.0
            perm[b + r, b + 8 + r] = 1.0
            invf[b + r] = invf[b + 8 + r] = inv[r]
            sgn[b + r], sgn[b + 8 + r] = -1.0, 1.0
    put("perm", perm)
    put("heads", np.stack([i < 64, i >= 64], 1))
    put("one", 1.0)
    put("invf", invf[:, None])
    put("sgn", sgn[:, None])
    put("half", -0.5)
    return c


class Line:

    def __init__(self, sem):
        self.sem, self.n, self.todo, self.seen = sem, 0, [], {}

    def wait(self, *marks):
        for m in marks:
            if m is not None and self.seen.get(id(m[0]), 0) < m[1]:
                self.seen[id(m[0])] = m[1]
                self.todo.append(lambda e, m=m: e.wait_ge(m[0], m[1]))

    def do(self, f, *marks):
        self.wait(*marks)
        self.todo.append(f)

    def mark(self, f, *marks):
        self.wait(*marks)
        self.n += 1
        self.todo.append(lambda e: f(e).then_inc(self.sem, 1))
        return (self.sem, self.n)

    def play(self, e):
        for f in self.todo:
            f(e)


class Buf:

    def __init__(self, ap):
        self.ap, self.after = ap, ()


class Store:

    def __init__(self, bufs):
        self.free = deque(bufs)
        self.least = len(self.free)

    def take(self, line):
        b = self.free.popleft()
        self.least = min(self.least, len(self.free))
        line.wait(*b.after)
        return b

    def give(self, b, *after):
        assert b not in self.free
        b.after = after
        self.free.append(b)

    def pick(self, b):
        self.free.remove(b)


def woven(main, side, every):
    n, left = 0, True
    for _ in main:
        n += 1
        while left and n >= every:
            n -= every
            left = next(side, None) is not None
        yield 1
    for _ in side:
        pass


def weave(main, side, every):
    run(woven(main, side, every))


def some(gen, n):
    for _ in range(n):
        if next(gen, None) is None:
            return
        yield 1


class Ahead:

    def __init__(self, items, gen):
        self.items, self.gen = items, gen

    def __getitem__(self, k):
        while len(self.items) <= k:
            next(self.gen)
        return self.items[k]


def run(gen):
    for _ in gen:
        pass


def program(nc, ctx, io, blocks, stop=None):
    def sem(name):
        return ctx.enter_context(nc.semaphore(name))

    sems = {n: sem(n) for n in ("s_pe", "s_act", "s_dve", "s_pool", "s_in", "s_pos", "s_out")}
    s_raw = [sem(f"s_raw{i}") for i in range(NRAW)]
    s_ada = [sem(f"s_ada{i}") for i in range(3)]
    s_ya = [sem(f"s_ya{i}") for i in range(KD)]
    s_x = [sem(f"s_x{i}") for i in range(KD)]
    ya_dram = nc.dram_tensor("ya", (KD, P, S), F, kind="Internal").ap()
    T, A, V, G, SP = (Line(sems.get(n)) for n in ("s_pe", "s_act", "s_dve", "s_pool", None))

    at = [-(-nc.sbuf_base // 64) * 64]

    def place(name, shape, dt=F, where=None):
        n = -(-4 * int(np.prod(shape[1:])) // 64) * 64
        h = nc.alloc_sbuf_tensor_at(name, shape, dt, offset=at[0] if where is None else where)
        if where is None:
            at[0] += n
        return h

    X = place("X", [P, KD, S])
    cst = place("cst", [P, NCONST])
    vec = place("vec", [P, NVEC])
    small = place("small", [P, 1400])
    raw = place("raw", [P, NRAW, 1024])
    whi = place("whi", [P, NW, 1024], R)
    wlo = place("wlo", [P, NW, 1024], R)
    hhi = place("hhi", [P, KD, S], R)
    hlo = place("hlo", [P, KD, S], R)
    early_at = at[0]
    ahi = place("ahi", [P, HALF, S], R)
    alo = place("alo", [P, HALF, S], R)
    triR = place("triR", [P, 256], R)
    slab_at = at[0]
    slab = place("slab", [P, NSLOT * S])
    pos = place("pos", [P, S], I32, where=slab_at + 16 * 4 * S)
    early = place("early", [P, HALF, 1024], where=early_at)
    early2 = place("early2", [P, 4, 1024], where=early_at - 16 * 1024)

    slots = [Buf(slab[:, i * S:(i + 1) * S]) for i in range(NSLOT)]
    tmp = Store(slots[:NSLOT - NADA])
    banks = Store([Buf(ctx.enter_context(nc.psum_tensor(f"pb{i}", [P, S], F))[:, :]) for i in range(8)])

    def C(name, a=0, n=None):
        o, w = CONST[name]
        return cst[:, o + a:o + (w if n is None else a + n)]

    def W(name, a=0, n=1):
        o, _ = VEC[name]
        return vec[:, o + a:o + a + n]

    ident = C("ident")
    used = [0]

    def cols(n):
        a = used[0]
        used[0] += n
        assert used[0] <= 1400
        return small[:, a:a + n]

    def rev(ap, pat, **kw):
        return ap.rearrange(pat, **kw)

    SP.do(lambda e: e.dma_start(cst[:, :], io["consts"]).then_inc(sems["s_in"], 16))
    SP.do(lambda e: e.dma_start(vec[:, :], io["vecs"]).then_inc(sems["s_in"], 16))
    SP.do(lambda e: e.dma_start(pos[:, :], io["positions"][0].partition_broadcast(P)).then_inc(sems["s_pos"], 16))
    got_in, got_pos = (sems["s_in"], 32), (sems["s_pos"], 16)
    xmark = []
    for k in range(KD):
        SP.do(lambda e, k=k: e.dma_start(X[:, k, :], io["xT"][k * P:(k + 1) * P, :]).then_inc(s_x[k], 16))
        xmark.append((s_x[k], 16))

    class Stream:
        loaded = split = used = 0
        done = {}
        halves = {}
        freed = {}

        def load(self):
            u = self.loaded
            if u >= UNITS:
                return
            self.loaded += 1
            r = u % NRAW
            SP.do(lambda e: e.dma_start(raw[:, r, :], io["stream"][u]).then_inc(s_raw[r], 16), self.freed.get(u - NRAW))

        def cut(self):
            u = self.split
            if u >= UNITS:
                return
            self.split += 1
            r, w = u % NRAW, u % NW
            landed = (s_raw[r], 16 * (u // NRAW + 1))
            hi = A.mark(lambda e: e.activation(whi[:, w, :], raw[:, r, :], ACT.Copy), landed, self.done.get(u - NW))
            lo = V.mark(lambda e: e.tensor_tensor(wlo[:, w, :], raw[:, r, :], whi[:, w, :].bitcast(F), ALU.subtract),
                        hi, self.done.get(u - NW))
            self.halves[u] = (hi, lo)
            self.freed[u] = lo
            self.load()

        def block(self, spec):
            n = len(blocks)
            blocks.append(spec)
            u, b = divmod(n, 8)
            if b == 0:
                T.wait(*self.halves[u])
            return u, u % NW, b

        def consumed(self, u, mark):
            self.done[u] = mark
            self.cut()

    st = Stream()

    def three(out, a, b, first, last):
        (ah, al), (bh, bl) = a, b
        T.do(lambda e: e.matmul(out, ah, bh, start=first, stop=False))
        T.do(lambda e: e.matmul(out, ah, bl, start=False, stop=False))
        return lambda e: e.matmul(out, al, bh, start=False, stop=last)

    def gemm(acts, K, outs, order="k", rows=P):
        M = len(outs)
        steps = [(k, m) for k in range(K) for m in range(M)] if order == "k" else [(k, m) for m in range(M) for k in range(K)]
        bank = {}
        for k, m in steps:
            name, col, evac = outs[m]
            if m not in bank:
                bank[m] = banks.take(T)
            u, w, b = st.block((name, k, col))
            hi, lo, marks = acts[k]
            T.wait(*marks)
            sl = slice(b * P, b * P + rows)
            f = three(bank[m].ap[:rows, :], (whi[:, w, sl], wlo[:, w, sl]), (hi, lo), k == 0, k == K - 1)
            if b == 7 or k == K - 1:
                mark = T.mark(f)
                if b == 7:
                    st.consumed(u, mark)
                if k == K - 1:
                    evac(bank[m], mark)
            else:
                T.do(f)
            yield 1

    def gemm_rows(acts, K, name, col, evac):
        bank = [banks.take(T) for _ in range(4)]
        for k in range(K):
            at4 = [st.block((name, k, col + P * j)) for j in range(4)]
            u, w, b = at4[0]
            hi, lo, marks = acts[k]
            T.wait(*marks)
            sl = slice(b * P, b * P + S)
            for t in range(4):
                ts = slice(t * P, t * P + P)
                f = three(bank[t].ap, (hi[:, ts], lo[:, ts]), (whi[:, w, sl], wlo[:, w, sl]), k == 0, k == K - 1)
                if t == 3 or k == K - 1:
                    mark = T.mark(f)
                    if t == 3 and b == 4:
                        st.consumed(u, mark)
                    if k == K - 1:
                        evac(t, bank[t], mark)
                else:
                    T.do(f)
                yield 1

    def halve(src, hi, lo, *ready):
        h = A.mark(lambda e: e.activation(hi, src, ACT.Copy), *ready)
        l = V.mark(lambda e: e.tensor_tensor(lo, src, hi.bitcast(F), ALU.subtract), h, *ready)
        return h, l

    class Stats:

        def __init__(self, width=1, ones=None):
            self.bank, self.n, self.wait, self.width = None, 0, [], width
            self.ones = C("one") if ones is None else ones

        def add(self, src, ready):
            sq = tmp.take(A)
            m = A.mark(lambda e: e.activation(sq.ap, src, ACT.Square), ready)
            self.wait.append((sq, m))
            return m

        def flush(self, keep=0, last=False):
            while len(self.wait) > keep:
                sq, m = self.wait.pop(0)
                if self.bank is None:
                    self.bank = banks.take(T)
                w, end = self.width, last and not self.wait
                for c in range(4):
                    f = (lambda e, c=c, first=self.n == 0 and c == 0, sq=sq, end=end:
                         e.matmul(self.bank.ap[:, w * c:w * c + w], sq.ap[:, c * P:(c + 1) * P], self.ones,
                                  start=first, stop=end, skip_group_check=True))
                    if c < 3:
                        T.do(f, m)
                    else:
                        self.mark = T.mark(f)
                        tmp.give(sq, self.mark)
                self.n += 1

        def scaled(self, scale, eps):
            self.flush(last=True)
            n = 4 * self.width
            v = cols(n)
            mv = V.mark(lambda e: e.tensor_scalar(v, self.bank.ap[:, 0:n], scale, eps, ALU.mult, ALU.add), self.mark)
            banks.give(self.bank, mv)
            self.v = v, mv

        def rsqrt(self, *a):
            if a:
                self.scaled(*a)
            (v, mv), n = self.v, 4 * self.width
            r = cols(n)
            return r, G.mark(lambda e: e.tensor_tensor(r, v, C("half", 0, n), ALU.pow), mv, got_in)

    def spread(r, ready, width=1):
        b = banks.take(T)
        n = P // width
        for i in range(4 * width):
            c, g = divmod(i, width)
            f = lambda e, c=c, g=g, i=i: e.matmul(b.ap[g * n:(g + 1) * n, c * P:(c + 1) * P],
                                                  r[:, i:i + 1].to_broadcast([P, n]), ident, start=True, stop=True)
            if i < 4 * width - 1:
                T.do(f, ready)
            else:
                m = T.mark(f)
        return b, m

    def normed(rstd, src, gain, shift, out, extra=(), then=None):
        b, mb = spread(*rstd)

        def one(k, x, ready, hi, lo):
            t = tmp.take(V)
            mt = V.mark(lambda e: e.scalar_tensor_tensor(t.ap, x, gain(k), b.ap, ALU.mult, ALU.mult), mb, ready, *extra)
            if shift is None:
                h, l = halve(t.ap, hi, lo, mt)
            else:
                h = A.mark(lambda e: e.activation(hi, t.ap, ACT.Identity, bias=shift(k)), mt, *extra)
                l = V.mark(lambda e: e.scalar_tensor_tensor(lo, t.ap, shift(k), hi.bitcast(F), ALU.add, ALU.subtract), h)
            tmp.give(t, h, l)
            return mt, (hi, lo, (h, l))

        done = []
        for k, (x, ready) in enumerate(src):
            done.append(one(k, x, ready, *out[k]))
            if then is not None:
                then(k)
        banks.give(b, done[-1][0])
        return [act for _, act in done]

    h_out = [(hhi[:, k, :], hlo[:, k, :]) for k in range(KD)]
    a_out = [(ahi[:, k, :], alo[:, k, :]) for k in range(HALF)]

    def residual(d, gate, stats, gmark=None):
        def evac(bank, mark):
            if gate is None:
                m = V.mark(lambda e: e.tensor_tensor(X[:, d, :], bank.ap, X[:, d, :], ALU.add), mark, xmark[d])
            else:
                m = V.mark(lambda e: e.scalar_tensor_tensor(X[:, d, :], bank.ap, gate(d), X[:, d, :], ALU.mult, ALU.add),
                           mark, xmark[d], gmark)
            xmark[d] = m
            banks.give(bank, m)
            if stats is not None:
                xmark[d] = m
                stats.flush(keep=1)
                stats.add(X[:, d, :], m)
        return evac

    cond = cols(8)
    mod = {(l, j): cols(8) for l in range(2) for j in range(6)}
    modmark = {}
    gs = {(l, j): cols(8) for l in range(2) for j in (1, 4)}
    m_cond = A.mark(lambda e: e.activation(cond, W("c", 0, 8), ACT.Silu), got_in)
    ada = [slab[:, (NSLOT - NADA + 2 * i) * S:(NSLOT - NADA + 2 * i + 2) * S] for i in range(4)]
    acc = ada[3]
    ada_n = [0]
    ada_free = {}
    s_early = []

    def ada_load(l, j, k):
        n = ada_n[0]
        ada_n[0] += 1
        i = n % 3
        SP.do(lambda e: e.dma_start(ada[i], io["ada_w"][l, k * P:(k + 1) * P, j * D:(j + 1) * D]).then_inc(s_ada[i], 16),
              ada_free.get(n - 3))
        return n, ada[i], (s_ada[i], 16 * (n // 3 + 1))

    def mod_finish(l, j, bank, mark):
        m = V.mark(lambda e: e.tensor_tensor(mod[l, j], bank.ap[:, 0:8], W("ada_b", 48 * l + 8 * j, 8), ALU.add), mark, got_in)
        banks.give(bank, m)
        if j in (1, 4):
            g = W("norm1" if j == 1 else "norm2", 8 * l, 8)
            m = V.mark(lambda e: e.scalar_tensor_tensor(gs[l, j], mod[l, j], 1.0, g, ALU.add, ALU.mult), m)
        modmark[l, j] = m

    def early_load(l, j, k):
        n = len(s_early)
        s_early.append(sem(f"s_early{n}"))
        a = early[:, n, :] if n < HALF else early2[:, n - HALF, :]
        SP.do(lambda e: e.dma_start(a, io["ada_w"][l, k * P:(k + 1) * P, j * D:(j + 1) * D]).then_inc(s_early[n], 16))
        return None, a, (s_early[n], 16)

    def mods_on_vector(which):
        acc_free = None
        order = [(l, j, k) for l, j in which for k in range(KD)]
        loads = deque(early_load(*o) for o in order[:16])
        ahead = deque(order[16:])
        for l, j in which:
            for k in range(KD):
                while ahead and len(loads) < 3:
                    loads.append(ada_load(*ahead.popleft()))
                n, a, landed = loads.popleft()
                if k == 0:
                    m = V.mark(lambda e, a=a: e.tensor_scalar(acc, a, cond[:, 0:1], None, ALU.mult), landed, m_cond, acc_free)
                else:
                    m = V.mark(lambda e, a=a, k=k: e.scalar_tensor_tensor(acc, a, cond[:, k:k + 1], acc, ALU.mult, ALU.add),
                               landed, m)
                if n is not None:
                    ada_free[n] = m
                yield 1
            bank = banks.take(T)
            for d in range(8):
                f = lambda e, d=d, bank=bank: e.matmul(bank.ap[:, d:d + 1], acc[:, d * P:(d + 1) * P], C("one"), start=(d == 0),
                                            stop=True, skip_group_check=True)
                if d < 7:
                    T.do(f, m)
                else:
                    acc_free = T.mark(f)
            mod_finish(l, j, bank, acc_free)
            yield 1
        for i in range(NSLOT - NADA, NSLOT):
            tmp.give(slots[i], acc_free, m)

    def first_stats():
        s = Stats()
        for d in range(KD):
            s.flush(keep=1)
            s.add(X[:, d, :], xmark[d])
        return s

    T.wait(got_in)
    V.wait(got_in)
    G.wait(got_in)
    stats = first_stats()
    mods = mods_on_vector([(0, 1), (0, 0), (0, 2), (0, 3), (0, 4), (0, 5)] + [(1, j) for j in range(6)])
    for _ in range(9):
        next(mods)
    stats.scaled(1.0 / D, EPS1)
    for _ in range(9):
        next(mods)
    for _ in range(NRAW):
        st.load()
    m_tri = V.mark(lambda e: e.tensor_copy(triR[:, :], cst[:, CONST["tri"][0]:CONST["tri"][0] + 256]))

    TWO_PI = 2.0 * np.pi
    C1 = 6.28125
    C2 = float(np.float32(round((TWO_PI - C1) * 2 ** 19) / 2 ** 19))
    C3 = float(TWO_PI - C1 - C2)
    MAGIC = 12582912.0

    def reduce_angle(ang, k, ready, scale, shift):
        m = G.mark(lambda e: e.tensor_scalar(k, ang, scale / TWO_PI, shift, ALU.mult, ALU.add), ready)
        m = G.mark(lambda e: e.tensor_scalar(k, k, MAGIC, None, ALU.add), m)
        m = G.mark(lambda e: e.tensor_scalar(k, k, -MAGIC, None, ALU.add), m)
        for c in (C1, C2, C3):
            m = G.mark(lambda e, c=c: e.tensor_scalar(part.ap, k, -c / scale, None, ALU.mult), m)
            m = G.mark(lambda e: e.tensor_tensor(ang, ang, part.ap, ALU.add), m)
        return m

    ang, ang2, turn, part, cosT, sinT = (tmp.take(G) for _ in range(6))
    m = G.mark(lambda e: e.tensor_copy(ang.ap, pos[:, :]), got_pos)
    slots[16].after = (m,)
    m = G.mark(lambda e: e.tensor_scalar(ang.ap, ang.ap, C("invf"), None, ALU.mult), m)
    m = reduce_angle(ang.ap, turn.ap, m, 1.0 / 4096, 0.0)
    m2 = G.mark(lambda e: e.tensor_copy(ang2.ap, ang.ap), m)
    rstd0 = stats.rsqrt()
    m2 = reduce_angle(ang2.ap, turn.ap, m2, 1.0, 0.25)
    m2 = G.mark(lambda e: e.tensor_scalar(ang2.ap, ang2.ap, float(np.pi / 2), None, ALU.add), m2)
    m = reduce_angle(ang.ap, turn.ap, m, 1.0, 0.0)
    LIM = 3.1415925
    m2 = G.mark(lambda e: e.tensor_scalar(ang2.ap, ang2.ap, LIM, -LIM, ALU.min, ALU.max), m2)
    m = G.mark(lambda e: e.tensor_scalar(ang.ap, ang.ap, LIM, -LIM, ALU.min, ALU.max), m)

    def x_src():
        return [(X[:, k, :], xmark[k]) for k in range(KD)]

    def mod_norm(stats, l, jg, js, then=None):
        return normed(rstd0 if stats is None else stats.rsqrt(1.0 / D, EPS1), x_src(), lambda k: gs[l, jg][:, k:k + 1], lambda k: mod[l, js][:, k:k + 1],
                      h_out, (modmark[l, jg], modmark[l, js]), then)

    def dump_x():
        for k in range(KD):
            SP.do(lambda e, k=k: e.dma_start(io["outT"][k * P:(k + 1) * P, :], X[:, k, :]).then_inc(sems["s_out"], 16), xmark[k])
        SP.wait((sems["s_out"], 16 * KD))

    def rope(src, ready):
        b = banks.take(T)
        mr = T.mark(lambda e: e.matmul(b.ap, C("perm"), src.ap, start=True, stop=True), ready)
        o, t = tmp.take(V), tmp.take(V)
        m1 = V.mark(lambda e: e.tensor_tensor(o.ap, src.ap, cosT.ap, ALU.mult), ready, *m_rope)
        m2 = V.mark(lambda e: e.tensor_tensor(t.ap, b.ap, sinT.ap, ALU.mult), mr)
        banks.give(b, m2)
        m3 = V.mark(lambda e: e.tensor_tensor(o.ap, o.ap, t.ap, ALU.add), m1, m2)
        tmp.give(t, m3)
        tmp.give(src, m3, mr)
        return o, m3

    def attention_a(acts):
        hold = {}

        def with_gain(gain, key):
            def evac(bank, mark):
                s = Stats(2, C("heads"))
                ms = s.add(bank.ap, mark)
                g = tmp.take(A)
                mg = A.mark(lambda e: e.activation(g.ap, bank.ap, ACT.Copy, scale=gain))
                banks.give(bank, mg, ms)
                hold[key] = (s, g, mg)
            return evac

        def plain(key):
            def evac(bank, mark):
                g = tmp.take(A)
                mg = A.mark(lambda e: e.activation(g.ap, bank.ap, ACT.Copy), mark)
                banks.give(bank, mg)
                hold[key] = (g, mg)
            return evac

        def keys():
            s, g, mg = hold["k"]
            r, mr = s.rsqrt(1.0 / 64, EPS1)
            yield 1
            o, mo = rope(g, mg)
            yield 1
            b, mb = spread(r, mr, 2)
            m = V.mark(lambda e: e.tensor_tensor(o.ap, o.ap, b.ap, ALU.mult), mb, mo)
            banks.give(b, m)
            hold["kr"] = (o, m)
            yield 1
            v, mv = hold["v"]
            bv = banks.take(T)
            for c in range(4):
                f = lambda e, c=c: e.transpose(bv.ap[:, c * P:(c + 1) * P], v.ap[:, c * P:(c + 1) * P], ident)
                if c < 3:
                    T.do(f, mv)
                else:
                    mt = T.mark(f)
            vn = tmp.take(A)
            m = A.mark(lambda e: e.activation(vn.ap, bv.ap, ACT.Copy), mt)
            banks.give(bv, m)
            tmp.give(v, mt)
            hold["vn"] = (vn, m)

        out_marks = []

        def query(t):
            s, g, mg = hold["q", t]
            r, mr = s.rsqrt(1.0, 64 * EPS1)
            q, mq = rope(g, mg)
            kr, mk = hold["kr"]
            vn, mvn = hold["vn"]
            box = {}

            def scores(i):
                lo = P if i == 0 else 0
                b = [banks.take(T), banks.take(T)]
                for h in range(2):
                    p = slice(64 * h, 64 * h + 64)
                    f = lambda e, p=p, h=h: e.matmul(b[h].ap[:, lo:256], q.ap[p, i * P:(i + 1) * P],
                                                     kr.ap[p, i * P - P + lo:(i + 1) * P], start=True, stop=True)
                    if h == 0:
                        T.do(f, mq, mk)
                    else:
                        ms = T.mark(f)
                if i == 3:
                    box["q_read"] = ms
                sm = tmp.take(V)
                mx, nm = cols(2), cols(2)
                marks = []
                for h in range(2):
                    sl = slice(256 * h + lo, 256 * h + 256)
                    marks.append(V.mark(lambda e, sl=sl, h=h: e.tensor_tensor_reduce(
                        sm.ap[:, sl], b[h].ap[:, lo:256], C("maskA", lo), 1.0, -3.0e38, ALU.add, ALU.max, mx[:, h:h + 1]), ms))
                    banks.give(b[h], marks[h])
                m = V.mark(lambda e: e.tensor_tensor(nm, mx, r[:, 2 * i:2 * i + 2], ALU.mult), marks[0], marks[1], mr)
                m = V.mark(lambda e: e.tensor_tensor(nm, nm, W("sinks", 2 * t, 2), ALU.max), m)
                m = V.mark(lambda e: e.tensor_scalar(nm, nm, -1.0, None, ALU.mult), m)
                box[i] = (lo, sm, nm, m)

            def exps(i):
                lo, sm, nm, m = box[i]
                den, es = cols(2), cols(2)
                for h in range(2):
                    sl = slice(256 * h + lo, 256 * h + 256)
                    A.do(lambda e, sl=sl, h=h: e.activation(
                        sm.ap[:, sl], sm.ap[:, sl], ACT.Exp, bias=nm[:, h:h + 1], scale=r[:, 2 * i + h:2 * i + h + 1],
                        accum_out=den[:, h:h + 1]), m, mr)
                    me = A.mark(lambda e, h=h: e.activation(es[:, h:h + 1], W("sinks", 2 * t + h), ACT.Exp, bias=nm[:, h:h + 1]))
                box[i] = (lo, sm, den, es, me)

            def weights(i):
                lo, sm, den, es, me = box[i]
                m = V.mark(lambda e: e.tensor_tensor(den, den, es, ALU.add), me)
                m = V.mark(lambda e: e.reciprocal(es, den), m)
                for h in range(2):
                    sl = slice(256 * h + lo, 256 * h + 256)
                    m2 = V.mark(lambda e, sl=sl, h=h: e.tensor_scalar(sm.ap[:, sl], sm.ap[:, sl], es[:, h:h + 1], None, ALU.mult), m)
                box[i] = (lo, sm, m2)

            def turned(i):
                lo, sm, m2 = box[i]
                b = banks.take(T)
                for h in range(2):
                    for c in range(lo // P, 2):
                        sl = slice(256 * h + P * c, 256 * h + P * c + P)
                        mt = T.mark(lambda e, sl=sl: e.transpose(b.ap[:, sl], sm.ap[:, sl], ident), m2)
                tmp.give(sm, mt)
                pT = tmp.take(A)
                src = rev(b.ap, "p (h l) -> p h l", h=2)[:, :, lo:]
                dst = rev(pT.ap, "p (h l) -> p h l", h=2)[:, :, lo:]
                mp = A.mark(lambda e: e.activation(dst, src, ACT.Copy), mt)
                banks.give(b, mp)
                box[i] = (lo, pT, mp)

            def values(i):
                lo, pT, mp = box[i]
                if i == 0:
                    box["o"] = banks.take(T)
                o = box["o"]
                for h in range(2):
                    for c in range(lo // P, 2):
                        kb = i - 1 + c
                        lhs = vn.ap[:, kb * P + 64 * h:kb * P + 64 * h + 64]
                        mo = T.mark(lambda e, lhs=lhs, h=h, c=c: e.matmul(
                            o.ap[64 * h:64 * h + 64, i * P:(i + 1) * P], lhs, pT.ap[:, 256 * h + P * c:256 * h + P * c + P],
                            start=(c == lo // P), stop=(c == 1)), mp, mvn)
                tmp.give(pT, mo)
                if i == 3:
                    hl = halve(o.ap, ahi[:, t, :], alo[:, t, :], mo)
                    banks.give(o, *hl)
                    tmp.give(q, box["q_read"])
                    out_marks.append((ahi[:, t, :], alo[:, t, :], hl))

            return [[lambda f=f, i=i: f(i) for f in (scores, exps, weights, turned, values)] for i in range(4)]

        flying = []

        def advance():
            for stage in (1, 2, 0, 3, 4):
                for it in list(flying):
                    if it[0] == stage:
                        it[1][stage]()
                        it[0] = -1 - stage
                        yield 1
            for it in list(flying):
                it[0] = -it[0]
                if it[0] == 5:
                    flying.remove(it)

        def side(tiles):
            ready = query(tiles[0])
            for t in tiles:
                now, ready = ready, None
                if now is None:
                    now = query(t)
                for i, item in enumerate(now):
                    flying.append([0, item])
                    yield from advance()
                    if i >= 2 and ready is None and ("q", t + 1) in hold:
                        ready = query(t + 1)
                        yield 1
            while flying:
                yield from advance()

        def group(tiles):
            return gemm(acts, KD, [("qkv_a", P * c, e) for c, e in tiles])

        def qtile(t):
            return (t, with_gain(W("qg"), ("q", t)))

        A.do(lambda e: e.preload_act_table_set("natural_log_exp_and_others"))
        run(group([(8, with_gain(W("kg"), "k")), (9, plain("v")), qtile(0)]))
        weave(woven(group([qtile(1), qtile(2)]), keys(), 2), mods_some(8), 2)
        rest = side(range(8))
        for ts in ((3, 4), (5, 6), (7,)):
            weave(woven(group([qtile(t) for t in ts]), some(rest, 16 * len(ts)), 0.5), mods_some(7 * len(ts)), 1.2)

        def done():
            for b, mk in ((hold["kr"][0], T), (hold["vn"][0], T), (cosT, V), (sinT, V)):
                tmp.give(b, (mk.sem, mk.n))

        def tail():
            yield from rest
            done()
        return Ahead(out_marks, tail())

    def project(acts, K, name, l, jg):
        s = Stats()
        gate = None if jg is None else (lambda d: mod[l, jg][:, d:d + 1])

        def all_():
            gm = None if jg is None else modmark[l, jg]
            yield from gemm(acts, K, [(name, P * d, residual(d, gate, s, gm)) for d in range(4)])
            if isinstance(acts, Ahead):
                run(acts.gen)
            yield from gemm(acts, K, [(name, P * d, residual(d, gate, s, gm)) for d in range(4, 8)], "m")
        run(all_())
        return s

    def mods_some(n):
        for _ in range(n or 0):
            if next(mods, None) is None:
                return
            yield 1

    def ffn(acts, l):
        s = Stats()
        gate = (lambda d: mod[l, 5][:, d:d + 1]) if l < 2 else None
        names = (f"gate{l}", f"up{l}", 0) if l < 2 else ("up", "up", DFF)
        seen = [None]
        for part, (f0, f1) in enumerate(((0, HALF), (HALF, KF))):
            marks = {}
            sg = {}

            def gate_evac(f):
                def evac(bank, mark):
                    if l == 2:
                        sg[f] = conv_silu(bank, mark, "fcw", 22, 3, f, W("fcb", f))
                        return
                    t = tmp.take(A)
                    sg[f] = (t, A.mark(lambda e: e.activation(t.ap, bank.ap, ACT.Silu), mark))
                    banks.give(bank, sg[f][1])
                return evac

            def up_evac(f):
                def evac(bank, mark):
                    t, mt = sg[f]
                    m = V.mark(lambda e: e.tensor_tensor(t.ap, t.ap, bank.ap, ALU.mult), mark, mt)
                    banks.give(bank, m)
                    hi, lo = a_out[f - f0]
                    hl = halve(t.ap, hi, lo, m, seen[0])
                    tmp.give(t, *hl)
                    marks[f] = (hi, lo, hl)
                return evac

            def grow():
                for f in range(f0, f1, 2):
                    ng, nu, o = names
                    yield from gemm(acts, KD, [(ng, P * f, gate_evac(f)), (ng, P * f + P, gate_evac(f + 1)),
                                               (nu, o + P * f, up_evac(f)), (nu, o + P * f + P, up_evac(f + 1))])
            weave(grow(), mods_some(200 if part else 30), 6)
            a = [marks[f] for f in range(f0, f1)]
            gm = modmark.get((l, 5))
            name = f"down{l}{part}"
            sp = s if part else None

            def fall():
                for d0, order in ((0, "k"), (4, "m" if part else "k")):
                    yield from gemm(a, f1 - f0, [(name, P * d, residual(d, gate, sp, gm)) for d in range(d0, d0 + 4)], order)
            weave(fall(), mods_some(200 if part else 16), 6)
            seen[0] = (T.sem, T.n)
        return s

    def conv_silu(bank, mark, name, tiles, width, i, bias):
        t = tmp.take(V)
        m = V.mark(lambda e: e.tensor_scalar(t.ap, bank.ap, W(name, (width - 1) * tiles + i), None, ALU.mult), mark)
        for d in range(1, width):
            m = V.mark(lambda e, d=d: e.scalar_tensor_tensor(t.ap[:, d:], bank.ap[:, :S - d], W(name, (width - 1 - d) * tiles + i),
                                                             t.ap[:, d:], ALU.mult, ALU.add), m)
        banks.give(bank, m)
        return t, A.mark(lambda e: e.activation(t.ap, t.ap, ACT.Silu, bias=bias), m)

    def stick(acts):
        hold, out_marks = {}, {}
        vals = {}

        def qk_evac(key, scale):
            def evac(bank, mark):
                g = tmp.take(A)
                mg = A.mark(lambda e: e.activation(g.ap, bank.ap, ACT.Copy, scale=scale), mark)
                banks.give(bank, mg)
                hold[key] = (g, mg)
            return evac

        def v_evac(half):
            def evac(t, bank, mark):
                g = tmp.take(A)
                mg = A.mark(lambda e: e.activation(g.ap, bank.ap, ACT.Copy), mark)
                banks.give(bank, mg)
                vals[half, t] = (g, mg)
            return evac

        def items(pairs):
            for t in pairs:
                for h in range(2):
                    for j in (3, 2, 1, 0):
                        yield t, h, j

        heads = {}

        def start(it):
            t, h, j = it
            w, p = S - P * j, slice(64 * h, 64 * h + 64)
            (q, mq), (k, mk) = hold["q", t], hold["k", t]
            b = banks.take(T)
            mz = T.mark(lambda e: e.matmul(b.ap[:, 0:w], k.ap[p, j * P:(j + 1) * P], q.ap[p, j * P:], start=True, stop=True,
                                           skip_group_check=True), mq, mk)
            if h == 1 and j == 0:
                tmp.give(q, mz)
                tmp.give(k, mz)
            e1 = tmp.take(A)
            m = A.mark(lambda e: e.activation(e1.ap[:, 0:w], b.ap[:, 0:w], ACT.Abs), mz)
            m = A.mark(lambda e: e.activation(e1.ap[:, 0:w], e1.ap[:, 0:w], ACT.Exp, scale=-1.0), m)
            m = A.mark(lambda e: e.activation(e1.ap[:, 0:w], e1.ap[:, 0:w], ACT.Ln, bias=1.0), m)
            m = V.mark(lambda e: e.scalar_tensor_tensor(e1.ap[:, 0:w], b.ap[:, 0:w], 0.0, e1.ap[:, 0:w], ALU.max, ALU.add), m)
            m = V.mark(lambda e: e.tensor_tensor(e1.ap[:, 0:P], e1.ap[:, 0:P], C("maskB"), ALU.mult), m)
            return b, e1, m, w

        def parts(it, state):
            b, e1, m, w = state
            n = parts_n[0] % 6
            parts_n[0] += 1
            hi, lo = (stk[i][:, n, 0:w] for i in range(2))
            ht = A.mark(lambda e: e.activation(hi, e1.ap[:, 0:w], ACT.Copy), m, parts_free.get(n))
            lt = V.mark(lambda e: e.tensor_tensor(lo, e1.ap[:, 0:w], hi.bitcast(F), ALU.subtract), ht)
            tmp.give(e1, ht, lt)
            return b, n, (ht, lt), w

        def sums(it, state):
            t, h, j = it
            b, n, hl, w = state
            if j == 3:
                heads[t, h] = []
            for jj, nn, ml in heads[t, h] + [(j, n, hl)]:
                tri = triR[:, 0:P] if jj == j else triR[:, P:2 * P]
                ww = S - P * jj
                for part in stk:
                    m = T.mark(lambda e, tri=tri, part=part, nn=nn, ww=ww: e.matmul(
                        b.ap[:, w - ww:w], tri, part[:, nn, 0:ww], start=False, stop=True, skip_group_check=True), *ml, m_tri)
                if j == 0:
                    parts_free[nn] = m
            heads[t, h].append((j, n, hl))
            a = tmp.take(A)
            ma = A.mark(lambda e: e.activation(a.ap[:, 0:w], b.ap[:, 0:w], ACT.Exp), m)
            banks.give(b, ma)
            ma = V.mark(lambda e: e.tensor_tensor(a.ap[:, 0:P], a.ap[:, 0:P], C("capB"), ALU.min), ma)
            return a, ma, w

        obank = {}

        def values(it, state):
            t, h, j = it
            a, ma, w = state
            if j == 3 and h == 0:
                obank[t] = banks.take(T)
            o = obank[t]
            v, mv = vals[t // 4, j]
            lhs = v.ap[:, (t % 4) * P + 64 * h:(t % 4) * P + 64 * h + 64]
            mo = T.mark(lambda e: e.matmul(o.ap[64 * h:64 * h + 64, S - w:], lhs, a.ap[:, 0:w], start=(j == 3), stop=(j == 0),
                                           skip_group_check=True), ma, mv)
            tmp.give(a, mo)
            if j == 0 and h == 1:
                hl = halve(o.ap, ahi[:, t, :], alo[:, t, :], mo)
                banks.give(o, *hl)
                out_marks[t] = (ahi[:, t, :], alo[:, t, :], hl)
                if t % 4 == 3:
                    for jj in range(4):
                        tmp.give(vals[t // 4, jj][0], mo)

        for b in slots[:12]:
            tmp.pick(b)
            A.wait(*b.after)
            V.wait(*b.after)
        stk = (stick_hi, stick_lo)
        parts_n, parts_free = [0], {}

        fly = []

        def advance():
            for f in list(fly):
                it, stage, state = f
                if stage == 1:
                    f[1:] = [2, parts(it, state)]
                elif stage == 2:
                    f[1:] = [3, sums(it, state)]
                elif stage == 3:
                    values(it, state)
                    fly.remove(f)

        def side(pairs):
            for it in items(pairs):
                advance()
                fly.append([it, 1, start(it)])
                yield 1

        def drain():
            while fly:
                advance()
                yield 1

        def qk(*ts):
            outs = []
            for t in ts:
                outs += [("qkv_b", P * t, qk_evac(("q", t), 0.125)), ("qkv_b", D + P * t, qk_evac(("k", t), 1.0))]
            return gemm(acts, KD, outs)

        def vrows(half):
            return gemm_rows(acts, KD, "qkv_b", 2 * D + S * half, v_evac(half))

        A.do(lambda e: e.preload_act_table_set("natural_log_exp_and_others"))
        run(vrows(0))
        run(qk(0))
        for t in range(1, 8):
            def main(t=t):
                if t == 4:
                    yield from vrows(1)
                yield from qk(t)
            weave(main(), side([t - 1]), 3 if t != 4 else 6)
        run(side([7]))
        run(drain())
        for b in slots[:12]:
            tmp.give(b, *parts_free.values())
        return [out_marks[t] for t in range(8)]

    def mixer(acts):
        held = {}

        def copied(key):
            def evac(bank, mark):
                t = tmp.take(A)
                m = A.mark(lambda e: e.activation(t.ap, bank.ap, ACT.Copy), mark)
                banks.give(bank, m)
                held[key] = (t, m)
            return evac

        ya_in = {}

        def v_evac(i):
            def evac(bank, mark):
                c, mc = held["c", i]
                m = V.mark(lambda e: e.tensor_tensor(c.ap, c.ap, bank.ap, ALU.mult), mc, mark)
                banks.give(bank, m)
                t = tmp.take(V)
                m = V.mark(lambda e: e.tensor_scalar(t.ap, c.ap, W("caw", 16 + i), None, ALU.mult), m)
                for d in (1, 2):
                    m = V.mark(lambda e, d=d: e.scalar_tensor_tensor(t.ap[:, d:], c.ap[:, :S - d], W("caw", 8 * (2 - d) + i),
                                                                     t.ap[:, d:], ALU.mult, ALU.add), m)
                tmp.give(c, m)
                held["cv", i] = (t, m)
            return evac

        def b_evac(i):
            def evac(bank, mark):
                t, mt = held["cv", i]
                m = V.mark(lambda e: e.tensor_tensor(t.ap, t.ap, bank.ap, ALU.mult), mt, mark)
                banks.give(bank, m)
                hl = halve(t.ap, *a_out[i], m)
                tmp.give(t, *hl)
                ya_in[i] = (*a_out[i], hl)
            return evac

        spilled = []

        def spill(i):
            def evac(bank, mark):
                t = tmp.take(A)
                m = A.mark(lambda e: e.activation(t.ap, bank.ap, ACT.Copy), mark)
                banks.give(bank, m)
                SP.do(lambda e: e.dma_start(ya_dram[i], t.ap).then_inc(s_ya[i], 16), m)
                spilled.append((s_ya[i], 16))
                tmp.give(t, (s_ya[i], 16))
            return evac

        for i in range(8):
            run(gemm(acts, KD, [("w_in", 3072 + P * i, copied(("c", i))), ("w_in", 4096 + P * i, v_evac(i)),
                                ("w_in", 2048 + P * i, b_evac(i))]))

        dtb = {}

        def dt_evac(bank, mark):
            v, u, ac = (tmp.take(V) for _ in range(3))
            n = slice(0, 32)
            neg = cols(1)
            m = V.mark(lambda e: e.tensor_scalar(v.ap[n, :], bank.ap[n, :], W("dtb")[n, :], None, ALU.add), mark)
            banks.give(bank, m)
            A.wait(*u.after)
            mu = A.mark(lambda e: e.activation(u.ap[n, :], v.ap[n, :], ACT.Abs), m)
            mu = A.mark(lambda e: e.activation(u.ap[n, :], u.ap[n, :], ACT.Exp, scale=-1.0), mu)
            ma = A.mark(lambda e: e.activation(neg[n, :], W("alog")[n, :], ACT.Exp))
            mu = A.mark(lambda e: e.activation(u.ap[n, :], u.ap[n, :], ACT.Ln, bias=1.0), mu)
            m = V.mark(lambda e: e.scalar_tensor_tensor(v.ap[n, :], v.ap[n, :], 0.0, u.ap[n, :], ALU.max, ALU.add), mu, m)
            mu = V.mark(lambda e: e.tensor_scalar(u.ap[n, :], v.ap[n, :], neg[n, :], -1.0, ALU.mult, ALU.mult), m, ma)
            for c in range(4):
                cs = slice(c * P, c * P + P)
                mc = V.mark(lambda e, cs=cs: e.tensor_tensor_scan(ac.ap[n, cs], ones32[n, cs], u.ap[n, cs], 0.0, ALU.mult, ALU.add),
                            mu, m_ones)
            b = banks.take(T)
            for c in range(4):
                cs = slice(c * P, c * P + P)
                T.do(lambda e, c=c, cs=cs: e.transpose(b.ap[:, 32 * c:32 * c + 32], v.ap[n, cs], ident[n, n]), m)
                T.do(lambda e, c=c, cs=cs: e.transpose(b.ap[:, P + 32 * c:P + 32 * c + 32], ac.ap[n, cs], ident[n, n]), mc)
                mt = T.mark(lambda e, c=c: e.matmul(b.ap[:, 256 + 32 * c:288 + 32 * c],
                                                    ac.ap[n, c * P + P - 1:c * P + P].to_broadcast([32, P]), ident[n, n],
                                                    start=True, stop=True))
            nat = tmp.take(A)
            m = A.mark(lambda e: e.activation(nat.ap[:, 0:384], b.ap[:, 0:384], ACT.Copy), mt)
            banks.give(b, m)
            tmp.give(v, mt)
            tmp.give(u, mc)
            dec = tmp.take(V)
            md = V.mark(lambda e: e.tensor_tensor(dec.ap[:, 0:P], nat.ap[:, 256:384], nat.ap[:, P:256], ALU.subtract), m)
            md = A.mark(lambda e: e.activation(dec.ap[:, 0:P], dec.ap[:, 0:P], ACT.Exp), md)
            me = A.mark(lambda e: e.activation(dec.ap[:, P:256], nat.ap[:, 256:384], ACT.Exp))
            dtb.update(ac=ac, mac=mc, nat=nat, mnat=m, dec=dec, mdec=(md, me), ends=[ac, nat, dec])

        ones = tmp.take(V)
        ones32 = ones.ap
        m_ones = V.mark(lambda e: e.memset(ones32, 1.0))
        run(gemm(acts, KD, [("dt", 0, dt_evac)], rows=32))
        tmp.give(ones, (V.sem, V.n))

        def ya_main():
            a = [ya_in[i] for i in range(8)]
            for d in (0, 4):
                yield from gemm(a, KD, [("w_a_out", P * (d + i), spill(d + i)) for i in range(4)])

        run(ya_main())
        ya_read = (T.sem, T.n)

        def xbc(i):
            def evac(bank, mark):
                held["x", i] = conv_silu(bank, mark, "scw", 24, 4, i, W("scb", i))
            return evac

        def xgroup(g):
            yield from gemm(acts, KD, [("w_in", 7168 + P * i, xbc(i)) for i in range(4 * g, 4 * g + 4)])
            yield from gemm(acts, KD, [("w_in", 7168 + P * i, xbc(i)) for i in (16 + g, 20 + g)])

        def per_head(ap, c, g):
            o = 32 * c + 8 * g
            return ap[:, o:o + 8].unsqueeze(2).to_broadcast([P, 8, 64])

        def h8(ap):
            return rev(ap, "p (h r) -> p h r", h=8)

        def four(f, ready):
            b = banks.take(T)
            for c in range(4):
                if c < 3:
                    T.do(lambda e, c=c: f(e, b.ap[:, c * P:(c + 1) * P], c), *ready)
                else:
                    m = T.mark(lambda e, c=c: f(e, b.ap[:, c * P:(c + 1) * P], c), *ready)
            return b, m

        def ssd(g):
            nat, mnat, dec, mdec, ac = dtb["nat"], dtb["mnat"], dtb["dec"], dtb["mdec"], dtb["ac"]
            xs = [held["x", i] for i in range(4 * g, 4 * g + 4)]
            (Bt, mB), (Ct, mC) = held["x", 16 + g], held["x", 20 + g]
            xd = []

            def x_rows(c):
                b, m = four(lambda e, o, j: e.transpose(o, xs[j][0].ap[:, c * P:(c + 1) * P], ident), [x[1] for x in xs])
                t = tmp.take(V)
                md = V.mark(lambda e: e.tensor_tensor(h8(t.ap), h8(b.ap), per_head(nat.ap, c, g), ALU.mult), m, mnat)
                banks.give(b, md)
                xd.append((t, md))

            for c in range(4):
                x_rows(c)
                yield 1
            bb, m = four(lambda e, o, c: e.transpose(o, Bt.ap[:, c * P:(c + 1) * P], ident), [mB])
            Bn = tmp.take(A)
            mBn = A.mark(lambda e: e.activation(Bn.ap, bb.ap, ACT.Copy), m)
            banks.give(bb, mBn)
            yield 1
            cbb, mm = four(lambda e, o, c: e.matmul(o, Bt.ap[:, c * P:(c + 1) * P], Ct.ap[:, c * P:(c + 1) * P], start=True, stop=True), [mB, mC])
            cb = tmp.take(V)
            c4 = lambda ap: rev(ap, "p (c l) -> p c l", c=4)
            mcb = V.mark(lambda e: e.tensor_tensor(c4(cb.ap), c4(cbb.ap), C("maskS").unsqueeze(1).to_broadcast([P, 4, P]), ALU.mult), mm)
            banks.give(cbb, mcb)
            tmp.give(Bt, mm)
            yield 1
            states = []

            def state(c):
                t = tmp.take(V)
                x, mx = xd[c]
                m = V.mark(lambda e: e.tensor_tensor(h8(t.ap), h8(x.ap), per_head(dec.ap, c, g), ALU.mult), mx, mdec[0])
                b = banks.take(T)
                m = T.mark(lambda e: e.matmul(b.ap, Bn.ap[:, c * P:(c + 1) * P], t.ap, start=True, stop=True), m, mBn)
                tmp.give(t, m)
                o = tmp.take(V)
                if c == 0:
                    mo = V.mark(lambda e: e.tensor_copy(o.ap, b.ap), m)
                else:
                    q, mq = states[-1]
                    mo = V.mark(lambda e: e.tensor_tensor(h8(o.ap), h8(q.ap), per_head(dec.ap[:, P:256], c, g), ALU.mult), mq, mdec[1])
                    mo = V.mark(lambda e: e.tensor_tensor(o.ap, o.ap, b.ap, ALU.add), mo, m)
                banks.give(b, mo)
                if c == 2:
                    tmp.give(Bn, m)
                states.append((o, mo))

            for c in range(3):
                state(c)
                yield 1

            def decays(h):
                H = 8 * g + h
                b = banks.take(T)
                m = T.mark(lambda e: e.matmul(b.ap, ident[0:32, H:H + 1].to_broadcast([32, P]), ac.ap[0:32, :], start=True, stop=True),
                           dtb["mac"])
                sg, ex = tmp.take(V), tmp.take(A)
                for c in range(4):
                    cs = slice(c * P, c * P + P)
                    ms = V.mark(lambda e, c=c, cs=cs: e.tensor_scalar(sg.ap[:, cs], b.ap[:, cs], nat.ap[:, P + 32 * c + H:P + 32 * c + H + 1],
                                                                      0.0, ALU.subtract, ALU.min), m, mnat)
                me = A.mark(lambda e: e.activation(ex.ap[:, P:], b.ap[:, P:], ACT.Exp), m, ms)
                banks.give(b, me)
                ms = A.mark(lambda e: e.activation(sg.ap, sg.ap, ACT.Exp), ms)
                ms = V.mark(lambda e: e.tensor_tensor(sg.ap, sg.ap, cb.ap, ALU.mult), ms, mcb)
                me = V.mark(lambda e: e.tensor_tensor(ex.ap[:, P:], ex.ap[:, P:], Ct.ap[:, P:], ALU.mult), me, mC)
                return sg, ms, ex, me

            ybank = {}

            def outputs(h, d):
                sg, ms, ex, me = d
                j, p = h // 2, slice(64 * (h % 2), 64 * (h % 2) + 64)
                hs = slice(64 * h, 64 * h + 64)
                if h % 2 == 0:
                    ybank[j] = banks.take(T)
                y = ybank[j]
                for c in range(4):
                    cs = slice(c * P, c * P + P)
                    x, mx = xd[c]
                    m = T.mark(lambda e, x=x, c=c, cs=cs: e.matmul(y.ap[p, cs], x.ap[:, hs], sg.ap[:, cs], start=True, stop=(c == 0)), ms, mx)
                    if c:
                        q, mq = states[c - 1]
                        m = T.mark(lambda e, q=q, cs=cs: e.matmul(y.ap[p, cs], q.ap[:, hs], ex.ap[:, cs], start=False, stop=True), me, mq)
                tmp.give(sg, m)
                tmp.give(ex, m)
                if h % 2:
                    x, mx = xs[j]
                    mo = V.mark(lambda e: e.scalar_tensor_tensor(x.ap, x.ap, W("skip", 4 * g + j), y.ap, ALU.mult, ALU.add), m, mx)
                    banks.give(y, mo)
                    held["y", 4 * g + j] = (x, mo)
                return m

            d = decays(0)
            yield 1
            for h in range(1, 8):
                nd = decays(h)
                yield 1
                outputs(h - 1, d)
                d = nd
                yield 1
            m = outputs(7, d)
            for x, _ in xd + states:
                tmp.give(x, m)
            tmp.give(cb, d[1])
            tmp.give(Ct, d[3])

        gstats, gacts = {}, {}

        def z_evac(i):
            def evac(bank, mark):
                y, my = held["y", i]
                t = tmp.take(A)
                m = A.mark(lambda e: e.activation(t.ap, bank.ap, ACT.Silu), mark)
                banks.give(bank, m)
                m = V.mark(lambda e: e.tensor_tensor(y.ap, y.ap, t.ap, ALU.mult), m, my)
                tmp.give(t, m)
                held["y", i] = (y, m)
                g = i // 4
                if i % 4 == 0:
                    gstats[g] = Stats()
                gstats[g].flush(keep=1)
                gstats[g].add(y.ap, m)
            return evac

        def zgroup(g):
            yield from gemm(acts, KD, [("w_in", 5120 + P * i, z_evac(i)) for i in range(4 * g, 4 * g + 4)])

        def gated(g, out, free=()):
            src = [held["y", i] for i in range(4 * g, 4 * g + 4)]
            ys = normed(gstats[g].rsqrt(1.0 / 512, EPS2), [(y.ap, m) for y, m in src], lambda j: W("snw", 4 * g + j), None, out, free)
            for (y, _), (_, _, hl) in zip(src, ys):
                tmp.give(y, *hl)
            gacts[g] = ys

        run(xgroup(0))

        def seg(g):
            if g >= 2:
                yield from zgroup(g - 2)
                gated(g - 2, a_out[4 * (g - 2):4 * (g - 2) + 4], (ya_read,))
            if g < 4:
                yield from xgroup(g)

        for g in range(1, 5):
            weave(seg(g), ssd(g - 1), 1.4 if g == 1 else 2.6)
        run(zgroup(3))
        for b in dtb["ends"]:
            tmp.give(b, (T.sem, T.n), (V.sem, V.n))

        ya = []

        def fetch(i):
            t = tmp.take(SP)
            SP.do(lambda e: e.dma_start(t.ap, ya_dram[i]).then_inc(s_ya[i], 16), spilled[i])
            ya.append((t, (s_ya[i], 32)))

        for i in range(8):
            fetch(i)
        mix = {}

        def gate_a(i):
            def evac(bank, mark):
                t = tmp.take(A)
                m = A.mark(lambda e: e.activation(t.ap, bank.ap, ACT.Sigmoid), mark)
                banks.give(bank, m)
                y, my = ya[i]
                mix["a", i] = (y, V.mark(lambda e: e.tensor_tensor(y.ap, y.ap, t.ap, ALU.mult), m, my))
                tmp.give(t, mix["a", i][1])
            return evac

        def gate_s(i):
            def evac(bank, mark):
                t = tmp.take(A)
                m = A.mark(lambda e: e.activation(t.ap, bank.ap, ACT.Sigmoid), mark)
                banks.give(bank, m)
                mix["s", i] = (t, m)
            return evac

        for fn, col in ((gate_a, 0), (gate_s, D)):
            for d in (0, 4):
                run(gemm(acts, KD, [("w_in", col + P * (d + i), fn(d + i)) for i in range(4)]))
        gated(3, h_out[0:4], ((T.sem, T.n),))
        merged = []

        def merge(i):
            def evac(bank, mark):
                t, mt = mix["s", i]
                y, my = mix["a", i]
                m = V.mark(lambda e: e.tensor_tensor(t.ap, t.ap, bank.ap, ALU.mult), mark, mt)
                banks.give(bank, m)
                m = V.mark(lambda e: e.tensor_tensor(t.ap, t.ap, y.ap, ALU.add), m, my)
                out = h_out[4 + i] if i < 4 else a_out[i - 4]
                hl = halve(t.ap, *out, m, mark)
                tmp.give(t, *hl)
                tmp.give(y, m)
                merged.append((*out, hl))
            return evac

        a = [x for g in range(4) for x in gacts[g]]
        for d in (0, 4):
            run(gemm(a, 16, [("w_s_out", P * (d + i), merge(d + i)) for i in range(4)]))
        return merged

    stick_hi = place("stick_hi", [P, 6, S], R, where=slab_at)
    stick_lo = place("stick_lo", [P, 6, S], R, where=slab_at + 6 * 4 * S)

    acts = mod_norm(None, 0, 1, 0, lambda k: st.cut() if k < NW else None)
    A.wait(*cosT.after, *sinT.after)
    m_cos = A.mark(lambda e: e.activation(cosT.ap, ang2.ap, ACT.Sin), m2)
    m = A.mark(lambda e: e.activation(sinT.ap, ang.ap, ACT.Sin), m)
    m_sin = G.mark(lambda e: e.tensor_scalar(sinT.ap, sinT.ap, C("sgn"), None, ALU.mult), m)
    m_rope = (m_cos, m_sin)

    for b in (ang, ang2, turn, part):
        tmp.give(b, m_cos, m_sin)
    if stop == "norm":
        for k in range(KD):
            hi, lo, mk = acts[k]
            xmark[k] = V.mark(lambda e, k=k, hi=hi, lo=lo: e.tensor_tensor(X[:, k, :], hi.bitcast(F), lo.bitcast(F), ALU.add), *mk)
        dump_x()
        return T, A, V, G, SP
    o = attention_a(acts)
    s = project(o, KD, "wo_a", 0, 2)
    if stop == "attn_a":
        dump_x()
        return T, A, V, G, SP
    s = ffn(mod_norm(s, 0, 4, 3), 0)
    run(mods)
    if stop == "l0":
        dump_x()
        return T, A, V, G, SP
    o = stick(mod_norm(s, 1, 1, 0))
    s = project(o, KD, "wo_b", 1, 2)
    if stop == "attn_b":
        dump_x()
        return T, A, V, G, SP
    s = ffn(mod_norm(s, 1, 4, 3), 1)

    merged = mixer(normed(s.rsqrt(1.0 / D, EPS2), x_src(), lambda k: W("mix", k), None, h_out))
    s = project(merged, KD, "w_o", 2, None)
    if stop == "mix":
        dump_x()
        return T, A, V, G, SP
    s = ffn(normed(s.rsqrt(1.0 / D, EPS2), x_src(), lambda k: W("ffn", k), None, h_out), 2)
    b, mb = spread(*s.rsqrt(1.0 / D, EPS2))

    def final(k):
        m = V.mark(lambda e: e.scalar_tensor_tensor(X[:, k, :], X[:, k, :], W("fin", k), b.ap, ALU.mult, ALU.mult), mb, xmark[k])
        SP.do(lambda e: e.dma_start(io["outT"][k * P:(k + 1) * P, :], X[:, k, :]).then_inc(sems["s_out"], 16), m)

    for k in range(KD):
        final(k)
    SP.wait((sems["s_out"], 16 * KD))
    assert len(blocks) == 8 * UNITS
    return T, A, V, G, SP


def bass_blocks_kernel(nc, io, blocks, stop=None):
    with ExitStack() as ctx:
        lines = program(nc, ctx, io, blocks, stop)
        block = ctx.enter_context(nc.Block())
        block.tensor(lines[0].play)
        block.scalar(lines[1].play)
        block.vector(lines[2].play)
        block.gpsimd(lines[3].play)
        block.sync(lines[4].play)


def layout(inputs, blocks):
    f = {n: np.asarray(a) for n, a in inputs.items()}
    heads = np.array([h * 64 + r for t in range(8) for h in (t, t + 8) for r in range(64)])
    qkv = f["wqkv_a"][0]
    w_in = f["w_in_2"][0]
    mats = {
        "qkv_a": np.concatenate([qkv[:, heads], qkv[:, D:]], 1), "wo_a": f["wo_a"][0][heads],
        "qkv_b": f["wqkv_b"][0], "wo_b": f["wo_b"][0], "w_in": w_in,
        "dt": np.concatenate([w_in[:, 10240:], np.zeros((D, 96), np.float32)], 1),
        "w_a_out": f["w_a_out_2"][0], "w_s_out": f["w_s_out_2"][0], "w_o": f["w_o_2"][0], "up": f["w_up_2"][0],
    }
    for l in range(2):
        mats[f"gate{l}"], mats[f"up{l}"] = f["w_gate"][l], f["w_up"][l]
        mats[f"down{l}0"], mats[f"down{l}1"] = f["w_down"][l][:HALF * P], f["w_down"][l][HALF * P:]
    mats["down20"], mats["down21"] = f["w_down_2"][0][:HALF * P], f["w_down_2"][0][HALF * P:]
    stream = np.zeros((UNITS, P, 1024), np.float32)
    for n, (name, k, c) in enumerate(blocks):
        stream[n // 8, :, (n % 8) * P:(n % 8 + 1) * P] = mats[name][k * P:(k + 1) * P, c:c + P]

    vec = np.zeros((P, NVEC), np.float32)

    def put(name, a):
        o, n = VEC[name]
        vec[:, o:o + n] = a

    def tiles(a):
        return a.reshape(-1, P).T

    put("c", tiles(f["c"]))
    put("ada_b", tiles(f["ada_b"]))
    put("norm1", tiles(f["norm1_g"]))
    put("norm2", tiles(f["norm2_g"]))
    put("qg", np.concatenate([f["q_norm_a"][0]] * 2)[:, None])
    put("kg", np.concatenate([f["k_norm_a"][0]] * 2)[:, None])
    order = np.array([h for t in range(8) for h in (t, t + 8)])
    put("sinks", np.broadcast_to(f["sinks_a"][0][order], (P, 16)))
    put("mix", tiles(f["norm_mix_w_2"]))
    put("ffn", tiles(f["norm_ffn_w_2"]))
    put("fin", tiles(f["final_norm_w_2"]))
    put("caw", tiles(f["conv_a_w_2"]))
    put("scw", tiles(f["ssd_conv_w_2"]))
    put("scb", tiles(f["ssd_conv_b_2"]))
    put("snw", tiles(f["ssd_norm_w_2"]))
    put("fcw", tiles(f["ffn_conv_w_2"]))
    put("fcb", tiles(f["ffn_conv_b_2"]))
    put("skip", tiles(np.repeat(f["d_skip_2"][0], 64)))
    for name in ("dtb", "alog"):
        o, _ = VEC[name]
        vec[:32, o] = f["dt_bias_2" if name == "dtb" else "a_log_2"][0]
    return {
        "xT": np.ascontiguousarray(f["x"][0].T), "positions": f["positions"], "ada_w": f["ada_w"],
        "consts": constants(), "vecs": vec, "stream": stream,
    }


SHAPES = {
    "xT": ((D, S), F), "positions": ((1, S), I32), "ada_w": ((2, D, 6 * D), F), "consts": ((P, NCONST), F),
    "vecs": ((P, NVEC), F), "stream": ((UNITS, P, 1024), F),
}


def kernel(**inputs):
    import concourse.bacc as _bacc
    from concourse.bass_utils import run_bass_kernel_spmd as _run

    nc = _bacc.Bacc("TRN2", target_bir_lowering=False, num_devices=1)
    io = {n: nc.dram_tensor(n, shape, dt, kind="ExternalInput").ap() for n, (shape, dt) in SHAPES.items()}
    io["outT"] = nc.dram_tensor("outT", (D, S), F, kind="ExternalOutput").ap()
    blocks = []
    bass_blocks_kernel(nc, io, blocks)
    r = _run(nc, [layout(inputs, blocks)], core_ids=[0])
    return np.ascontiguousarray(r.results[0]["outT"].T)[None]
```
